# Optimizing a Trainium2 kernel written in Bass

```python
import jax, jax.numpy as jnp
from jax import lax
import numpy as np

D_MODEL = 1024
BATCH = 1
SEQ = 512
DEPTH = 1

CHUNK = 64
Q_BLOCK = 128
FOX_HEADS = D_MODEL // 128
FOX_HD = 64
FOX_W = FOX_HEADS * FOX_HD
ML_HEADS = 4
ML_HD = D_MODEL // 8
ML_W = ML_HEADS * ML_HD
CONV_K = 4
N_MEM = 256
X_HEADS = 4
X_HD = D_MODEL // X_HEADS
D_FF = 4 * D_MODEL
N_BRANCH = 2
EPS = 1e-6
SPLIT_SIZES = (FOX_W, FOX_W, FOX_W, FOX_HEADS,
               2 * ML_W, ML_W, ML_W, ML_HEADS, ML_HEADS,
               N_BRANCH * D_MODEL)
IN_WIDTH = sum(SPLIT_SIZES)
SPLIT_POINTS = tuple(int(s) for s in np.cumsum(SPLIT_SIZES)[:-1])

kernel_name = "hybrid_fox_mlstm_gated_trunk"

def rms_norm(x, g):
    xf = x.astype(jnp.float32)
    y = xf * lax.rsqrt(jnp.mean(xf * xf, axis=-1, keepdims=True) + EPS)
    return (y * g.astype(jnp.float32)).astype(x.dtype)

def causal_conv(u, w, b):
    S = u.shape[1]
    up = jnp.pad(u, ((0, 0), (CONV_K - 1, 0), (0, 0)))
    out = b
    for j in range(CONV_K):
        out = out + w[j] * up[:, j:j + S]
    return out

def fox_attention(q, k, v, fpre):
    B, S, H, d = q.shape
    nq = S // Q_BLOCK
    f32 = jnp.float32
    qf = q.astype(f32).transpose(0, 2, 1, 3) * (d ** -0.5)
    kf = k.astype(f32).transpose(0, 2, 1, 3)
    vf = v.astype(f32).transpose(0, 2, 1, 3)
    c = jnp.cumsum(jax.nn.log_sigmoid(fpre.astype(f32)), axis=1).transpose(0, 2, 1)
    qb = qf.reshape(B, H, nq, Q_BLOCK, d).transpose(2, 0, 1, 3, 4)
    cb = c.reshape(B, H, nq, Q_BLOCK).transpose(2, 0, 1, 3)
    kpos = jnp.arange(S)

    def block(args):
        qi, ci, i = args
        qpos = i * Q_BLOCK + jnp.arange(Q_BLOCK)
        logits = jnp.einsum('bhqd,bhkd->bhqk', qi, kf) + ci[..., :, None] - c[..., None, :]
        logits = jnp.where(kpos[None, :] <= qpos[:, None], logits, -jnp.inf)
        p = jax.nn.softmax(logits, axis=-1)
        return jnp.einsum('bhqk,bhkd->bhqd', p, vf)

    o = lax.map(block, (qb, cb, jnp.arange(nq)))
    return o.transpose(1, 0, 3, 2, 4).reshape(B, S, H * d)

def mlstm_chunkwise(q, k, v, ipre, fpre):
    B, S, H, d = q.shape
    L = CHUNK
    nc = S // L
    f32 = jnp.float32
    def chunked(t):
        return t.astype(f32).transpose(0, 2, 1, 3).reshape(B, H, nc, L, d)
    qc, kc, vc = chunked(q), chunked(k) * (d ** -0.5), chunked(v)
    ig = ipre.astype(f32).transpose(0, 2, 1).reshape(B, H, nc, L)
    logf = jax.nn.log_sigmoid(fpre.astype(f32)).transpose(0, 2, 1).reshape(B, H, nc, L)
    bcum = jnp.cumsum(logf, axis=-1)
    bL = bcum[..., -1]
    a = bL[..., None] - bcum + ig
    m_loc = jnp.max(a, axis=-1)
    wloc = jnp.exp(a - m_loc[..., None])
    C_loc = jnp.einsum('bhcl,bhcld,bhcle->bhcde', wloc, kc, vc)
    n_loc = jnp.einsum('bhcl,bhcld->bhcd', wloc, kc)

    def step(carry, xs):
        C, n, m = carry
        bl, ml, Cl, nl = xs
        m_new = jnp.maximum(bl + m, ml)
        s_old = jnp.exp(bl + m - m_new)
        s_loc = jnp.exp(ml - m_new)
        C_new = s_old[..., None, None] * C + s_loc[..., None, None] * Cl
        n_new = s_old[..., None] * n + s_loc[..., None] * nl
        return (C_new, n_new, m_new), (C, n, m)

    init = (jnp.zeros((B, H, d, d), f32), jnp.zeros((B, H, d), f32), jnp.zeros((B, H), f32))
    xs = (jnp.moveaxis(bL, 2, 0), jnp.moveaxis(m_loc, 2, 0),
          jnp.moveaxis(C_loc, 2, 0), jnp.moveaxis(n_loc, 2, 0))
    _, (C_prev, n_prev, m_prev) = lax.scan(step, init, xs)
    C_prev = jnp.moveaxis(C_prev, 0, 2)
    n_prev = jnp.moveaxis(n_prev, 0, 2)
    m_prev = jnp.moveaxis(m_prev, 0, 2)

    tri = jnp.tril(jnp.ones((L, L), dtype=bool))
    Dlog = bcum[..., :, None] - bcum[..., None, :] + ig[..., None, :]
    Dlog = jnp.where(tri, Dlog, -jnp.inf)
    inter_log = bcum + m_prev[..., None]
    m_t = jnp.maximum(inter_log, jnp.max(Dlog, axis=-1))
    Dw = jnp.exp(Dlog - m_t[..., None])
    inter_w = jnp.exp(inter_log - m_t)
    sqk = jnp.einsum('bhcld,bhcsd->bhcls', qc, kc) * Dw
    num = inter_w[..., None] * jnp.einsum('bhcld,bhcde->bhcle', qc, C_prev) \
        + jnp.einsum('bhcls,bhcse->bhcle', sqk, vc)
    den = inter_w * jnp.einsum('bhcld,bhcd->bhcl', qc, n_prev) + jnp.sum(sqk, axis=-1)
    h = num / jnp.maximum(jnp.abs(den), jnp.exp(-m_t))[..., None]
    return h.reshape(B, H, S, d).transpose(0, 2, 1, 3)

def cross_attention(hn, memn, wq, wkv, wo):
    B, S, _ = hn.shape
    q = (hn @ wq).reshape(B, S, X_HEADS, X_HD)
    kv = memn @ wkv
    k, v = jnp.split(kv, 2, axis=-1)
    k = k.reshape(B, -1, X_HEADS, X_HD)
    v = v.reshape(B, -1, X_HEADS, X_HD)
    logits = jnp.einsum('bqhd,bkhd->bhqk', q, k).astype(jnp.float32) * (X_HD ** -0.5)
    p = jax.nn.softmax(logits, axis=-1).astype(v.dtype)
    o = jnp.einsum('bhqk,bkhd->bqhd', p, v).reshape(B, S, D_MODEL)
    return o @ wo

def setup_inputs(seed: int = 0) -> dict:
    key = jax.random.key(seed)
    ks = jax.random.split(key, 32)
    f32 = jnp.float32
    def nrm(k, shape, fan_in):
        return jax.random.normal(k, shape, f32) * (fan_in ** -0.5)
    def gain(k, shape):
        return 1.0 + 0.02 * jax.random.normal(k, shape, f32)
    return {
        "x": jax.random.normal(ks[0], (BATCH, SEQ, D_MODEL), f32),
        "mem": jax.random.normal(ks[1], (BATCH, N_MEM, D_MODEL), f32),
        "norm_mix": gain(ks[2], (DEPTH, D_MODEL)),
        "norm_xattn": gain(ks[3], (DEPTH, D_MODEL)),
        "norm_mem": gain(ks[4], (DEPTH, D_MODEL)),
        "norm_mlp": gain(ks[5], (DEPTH, D_MODEL)),
        "w_in": nrm(ks[6], (DEPTH, D_MODEL, IN_WIDTH), D_MODEL),
        "b_fox_f": jax.random.uniform(ks[7], (DEPTH, FOX_HEADS), f32, 2.0, 5.0),
        "b_mlstm_i": 0.1 * jax.random.normal(ks[8], (DEPTH, ML_HEADS), f32),
        "b_mlstm_f": jax.random.uniform(ks[9], (DEPTH, ML_HEADS), f32, 3.0, 6.0),
        "b_gate": 0.01 * jax.random.normal(ks[10], (DEPTH, N_BRANCH * D_MODEL), f32),
        "conv_w": nrm(ks[11], (DEPTH, CONV_K, 2 * ML_W), CONV_K),
        "conv_b": 0.01 * jax.random.normal(ks[12], (DEPTH, 2 * ML_W), f32),
        "mlstm_norm": gain(ks[13], (DEPTH, ML_W)),
        "w_up_fox": nrm(ks[14], (DEPTH, FOX_W, D_MODEL), FOX_W),
        "w_up_mlstm": nrm(ks[15], (DEPTH, ML_W, D_MODEL), ML_W),
        "w_mix_out": nrm(ks[16], (DEPTH, D_MODEL, D_MODEL), D_MODEL),
        "w_xq": nrm(ks[17], (DEPTH, D_MODEL, D_MODEL), D_MODEL),
        "w_xkv": nrm(ks[18], (DEPTH, D_MODEL, 2 * D_MODEL), D_MODEL),
        "w_xo": nrm(ks[19], (DEPTH, D_MODEL, D_MODEL), D_MODEL),
        "w_mlp_in": nrm(ks[20], (DEPTH, D_MODEL, D_FF), D_MODEL),
        "w_mlp_out": nrm(ks[21], (DEPTH, D_FF, D_MODEL), D_FF),
        "norm_final": gain(ks[22], (D_MODEL,)),
    }

def reference(x, mem, norm_mix, norm_xattn, norm_mem, norm_mlp, w_in, b_fox_f, b_mlstm_i,
              b_mlstm_f, b_gate, conv_w, conv_b, mlstm_norm, w_up_fox, w_up_mlstm, w_mix_out,
              w_xq, w_xkv, w_xo, w_mlp_in, w_mlp_out, norm_final):
    B, S, _ = x.shape
    h = x
    for l in range(DEPTH):
        xn = rms_norm(h, norm_mix[l])
        proj = xn @ w_in[l]
        fq, fk, fv, ff, mqk, mv, mo, mi, mf, gpre = jnp.split(proj, SPLIT_POINTS, axis=-1)
        y_fox = fox_attention(fq.reshape(B, S, FOX_HEADS, FOX_HD),
                              fk.reshape(B, S, FOX_HEADS, FOX_HD),
                              fv.reshape(B, S, FOX_HEADS, FOX_HD),
                              ff + b_fox_f[l]).astype(h.dtype)
        qk = jax.nn.silu(causal_conv(mqk, conv_w[l], conv_b[l]))
        mq, mk = jnp.split(qk, 2, axis=-1)
        hm = mlstm_chunkwise(mq.reshape(B, S, ML_HEADS, ML_HD),
                             mk.reshape(B, S, ML_HEADS, ML_HD),
                             mv.reshape(B, S, ML_HEADS, ML_HD),
                             mi + b_mlstm_i[l], mf + b_mlstm_f[l])
        hm = hm * lax.rsqrt(jnp.mean(hm * hm, axis=-1, keepdims=True) + EPS)
        hm = hm.reshape(B, S, ML_W) * mlstm_norm[l].astype(jnp.float32)
        y_ml = (hm * jax.nn.sigmoid(mo.astype(jnp.float32))).astype(h.dtype)
        g = jax.nn.sigmoid(gpre + b_gate[l])
        g_fox, g_ml = jnp.split(g, 2, axis=-1)
        merged = g_fox * (y_fox @ w_up_fox[l]) + g_ml * (y_ml @ w_up_mlstm[l])
        h = h + merged @ w_mix_out[l]
        hn = rms_norm(h, norm_xattn[l])
        memn = rms_norm(mem, norm_mem[l])
        h = h + cross_attention(hn, memn, w_xq[l], w_xkv[l], w_xo[l])
        hn = rms_norm(h, norm_mlp[l])
        a = jax.nn.relu(hn @ w_mlp_in[l])
        h = h + (a * a) @ w_mlp_out[l]
    return rms_norm(h, norm_final)


_drawn_inputs = setup_inputs


def setup_inputs(seed=0):
    import zlib

    import numpy as np

    out = dict(_drawn_inputs(seed))
    spreads = {}
    factors = {'norm_mix': 4.647,
     'norm_xattn': 8.0,
     'norm_mem': 8.0,
     'norm_mlp': 9.179,
     'b_mlstm_i': 64.0,
     'b_gate': 8.0,
     'conv_b': 24.327,
     'mlstm_norm': 8.0,
     'norm_final': 22.46}
    for name, (base, spread) in spreads.items():
        noise = np.random.default_rng([zlib.crc32(name.encode()), seed]).standard_normal(out[name].shape)
        drawn = base * np.exp(spread * noise) if base else spread * noise
        out[name] = __import__('jax').numpy.asarray(drawn.astype(out[name].dtype))
    for name, factor in factors.items():
        out[name] = (out[name] * factor).astype(out[name].dtype)
    return out
```

```python
from contextlib import ExitStack

import concourse.bass as bass
from concourse import mybir

F32 = mybir.dt.float32
F32R = mybir.dt.float32r
BF16 = mybir.dt.bfloat16
I32 = mybir.dt.int32
ALU = mybir.AluOpType
ACT = mybir.ActivationFunctionType
AX_X = mybir.AxisListType.X

P = 128
TOK = 512
NT = TOK // P
DM = 1024
KT = DM // P
FF = 4 * DM
MEM = 256
FOX_HEADS, FOX_HD = 8, 64
ML_HEADS, ML_HD = 4, 128
X_HEADS, X_HD = 4, 256
HALF_W = 512
CONV_K = 4
EPS = 1e-6
HIDE = -1e30

C_FQ, C_FK, C_FV, C_FF = 0, 512, 1024, 1536
C_MQ, C_MK, C_MV, C_MO, C_MI, C_GF, C_GM = 1544, 2056, 2568, 3080, 3592, 3600, 4624

RING = 12
LOT = 4
STAGES = 2

WARM_UP = 20
N_FOX = FOX_HEADS * NT
N_ML = ML_HEADS * NT
N_X = X_HEADS * NT
ML0, X0 = N_FOX, N_FOX + N_ML
KB = 1024


def make_units():
    u = [
        ("fox_v", "w_in", 0, KT, C_FV, NT),
        ("fox_q", "w_in", 0, KT, C_FQ, 4),
        ("fox_k", "w_in", 0, KT, C_FK, 4),
        ("conv_q", "w_in", 0, KT, C_MQ, 4),
        ("conv_k", "w_in", 0, KT, C_MK, 4),
        ("ml_v", "w_in", 0, KT, C_MV, NT),
        ("ml_o", "w_in", 0, KT, C_MO, 4),
        ("gate_fox0", "w_in", 0, KT, C_GF, 4),
        ("gate_ml0", "w_in", 0, KT, C_GM, 4),
        ("gate_fox1", "w_in", 0, KT, C_GF + HALF_W, 4),
        ("up_fox0", "w_up_fox", 0, 4, 0, 4),
        ("up_ml0", "w_up_mlstm", 0, 4, 0, 4),
        ("gate_ml1", "w_in", 0, KT, C_GM + HALF_W, 4),
        ("up_fox1", "w_up_fox", 0, 4, HALF_W, 4),
        ("up_ml1", "w_up_mlstm", 0, 4, HALF_W, 4),
        ("mix0", "w_mix_out", 0, KT, 0, NT),
        ("mix1", "w_mix_out", 0, KT, HALF_W, NT),
        ("mem_k0", "w_xkv", 0, KT, 0, 4),
        ("mem_k1", "w_xkv", 0, KT, HALF_W, 4),
        ("x_q0", "w_xq", 0, KT, 0, 4),
        ("x_q1", "w_xq", 0, KT, HALF_W, 4),
        ("mem_v0", "w_xkv", 0, KT, DM, MEM // P),
        ("mem_v1", "w_xkv", 0, KT, DM + HALF_W, MEM // P),
        ("x_out0", "w_xo", 0, KT, 0, NT),
        ("x_out1", "w_xo", 0, KT, HALF_W, NT),
    ]
    for r in range(FF // DM):
        u += [
            (f"mlp_in{2 * r}", "w_mlp_in", 0, KT, r * DM, 4),
            (f"mlp_in{2 * r + 1}", "w_mlp_in", 0, KT, r * DM + HALF_W, 4),
            (f"mlp_out{2 * r}", "w_mlp_out", r * DM, KT, 0, NT),
            (f"mlp_out{2 * r + 1}", "w_mlp_out", r * DM, KT, HALF_W, NT),
        ]
    return u


UNITS = make_units()
UNIT = {u[0]: n for n, u in enumerate(UNITS)}
SLAB0 = [sum(u[3] for u in UNITS[:n]) for n in range(len(UNITS) + 1)]
GROUP0 = [sum(u[5] for u in UNITS[:n]) for n in range(len(UNITS) + 1)]


def make_halves():
    halves = []
    for n, u in enumerate(UNITS):
        cs, groups = range(u[3] // 4), range(u[5])
        if u[0] == "mlp_in0":
            halves += [(n, j, c, 0, TOK - P) for j in (0, 1) for c in cs]
            halves += [(n, j, c, TOK - P, TOK) for j in (0, 1) for c in cs]
            groups = groups[2:]
        width = MEM if u[0].startswith("mem_k") else TOK
        halves += [(n, j, c, 0, width) for j in groups for c in cs]
    return halves


HALVES = make_halves()
HALF_AT = {h[:3]: i for i, h in enumerate(HALVES)}
FIRST_HALF = {h[0]: i for i, h in reversed(list(enumerate(HALVES)))}


def group_end(n, j):
    return HALF_AT[(n, j, UNITS[n][3] // 4 - 1)] + 1


def kind(n):
    return UNITS[n][0].rstrip("0123456789")


def order(n):
    return int(UNITS[n][0][len(kind(n)):] or 0)


def by_tokens(n):
    return kind(n) in ("fox_v", "ml_v", "mix", "mem_v", "x_out", "mlp_out")


def free_after(pair):
    s = 2 * pair + 1 - RING
    if s < 0:
        return -1
    n = max(i for i in range(len(UNITS)) if SLAB0[i] <= s)
    return HALF_AT[(n, UNITS[n][5] - 1, (s - SLAB0[n]) // 4)]


def make_steps():
    steps = []
    at = {}

    def before(h, *what):
        at.setdefault(h, ([], []))[0].extend(what)

    def after(h, *what):
        at.setdefault(h, ([], []))[1].extend(what)

    def first(name):
        return FIRST_HALF[UNIT[name]]

    steps += [("norm", 0), ("split_weights", 0), ("norm_turn", 0), ("norm_split", 0), ("split_weights", 1),
              ("norm", 1), ("split_weights", 2), ("split_weights", 3)]
    after(1, ("norm_turn", 1), ("norm_split", 1), ("norm", 2))
    after(2, ("norm_turn", 2), ("norm_split", 2), ("norm", 3))
    after(4, ("norm_turn", 3), ("norm_split", 3), ("split_weights", 4), ("split_weights", 5))
    before(first("fox_q") + 2, ("parameters", 0))
    before(first("fox_q") + 4, ("gates", 0))
    after(first("fox_q") + 4, ("gate_rows", 0))
    before(first("fox_k") - 2, ("gate_turn", 0))
    before(first("conv_q") - 4, ("decay", 0))

    h0 = first("conv_q") - 1
    place = [h0 + t + (2 if t >= ML0 else 0) for t in range(X0)]
    for t in range(X0):
        before(place[t] + 4, ("values", t))
    for t in range(X0):
        before(place[t] + 2, ("turn", t))
    for t in range(X0):
        before(place[t], ("scores", t))
        after(place[t], ("probs", t))
    for t in range(X0):
        after(place[t] + 2, ("turned", t))
    for c in range(KT):
        g = group_end(UNIT["conv_q" if c < 4 else "conv_k"], c % 4) - 1
        after(g + 1, ("conv_tanh", c))
        after(g + 2, ("conv_silu", c))
    for t in range(2 * NT - 1, ML0, 2 * NT):
        after(place[t] + 4, ("fox_split", t // (2 * NT)))
    for h in range(ML_HEADS):
        w = place[ML0 + NT * h + NT - 1] + 4
        after(w, ("ml_quotient", h))
        after(w + 1, ("ml_squares", h))
        after(w + 2, ("ml_norm", h))
        before(w + 4, ("ml_turn", h))
        after(w + 4, ("ml_split", h))

    for m in range(4):
        after(first("up_fox1") + m, ("merge_split", m))
    for m in range(4, KT):
        after(first("up_ml1") + m - 4, ("merge_split", m))

    h = first("mix0")
    for i in range(MEM // P):
        after(h + 2 * i + 2, ("norm", NT + i))
        after(h + 2 * i + 4, ("norm_turn", NT + i), ("norm_split", NT + i))
    for unit, n0, last in (("mix1", NT + 2, 5), ("x_out1", 2 * NT + 2, 3)):
        n = UNIT[unit]
        for i in range(NT):
            g = group_end(n, i) - 1
            after(g, ("norm", n0 + i))
            after(g + (2 if i < NT - 1 else last), ("norm_turn", n0 + i), ("norm_split", n0 + i))
    n = UNIT[f"mlp_out{2 * FF // DM - 1}"]
    for i in range(NT):
        after(group_end(n, i) - 1, ("norm", 3 * NT + 2 + i))

    hx = first("x_q1")
    for t in range(N_X):
        w = hx + t if t < N_X // 2 else hx + N_X // 2 + 5 * (t - N_X // 2) // 8
        before(w + 1, ("turn", X0 + t))
        after(w + 1, ("turned", X0 + t))
        before(w, ("scores", X0 + t))
        after(w, ("probs", X0 + t))
    for h, w in enumerate((first("mem_v1"), first("mem_v1") + 1, first("x_out0"), first("x_out0"))):
        before(w, ("x_values", h))
        after(w, ("x_split", h))

    pairs = {}
    for pair in range(RING // 2, SLAB0[-1] // 2):
        f = free_after(pair)
        n = max(i for i in range(len(UNITS)) if SLAB0[i] <= 2 * pair)
        need = FIRST_HALF[n] + (2 * pair - SLAB0[n]) // 4
        pairs.setdefault(max(f, min(f + 1, need - 2)), []).append(pair)

    for i, (n, j, c, *_) in enumerate(HALVES):
        b, a = at.pop(i, ([], []))
        steps += b + [("half", i)]
        steps += [("split_weights", p) for p in pairs.get(i, []) if p % 4 >= 2]
        soon = [x for x in a if x[0] in ("probs", "turned", "conv_tanh", "conv_silu", "split_weights")]
        steps += soon
        if c == UNITS[n][3] // 4 - 1 and HALF_AT[(n, j, c)] == i:
            steps.append(("take", GROUP0[n] + j))
        steps += [x for x in a if x not in soon]
        steps += [("split_weights", p) for p in pairs.get(i, []) if p % 4 < 2]
    assert not at, at
    return steps


def trunk(nc, x, mem, norm_mix, norm_xattn, norm_mem, norm_mlp, w_in, b_fox_f, b_mlstm_i, b_mlstm_f,
          b_gate, conv_w, conv_b, mlstm_norm, w_up_fox, w_up_mlstm, w_mix_out, w_xq, w_xkv, w_xo,
          w_mlp_in, w_mlp_out, norm_final, out):
    weights = {"w_in": w_in, "w_up_fox": w_up_fox, "w_up_mlstm": w_up_mlstm, "w_mix_out": w_mix_out,
               "w_xq": w_xq, "w_xkv": w_xkv, "w_xo": w_xo, "w_mlp_in": w_mlp_in, "w_mlp_out": w_mlp_out}
    steps = make_steps()

    with ExitStack() as ctx:
        def sem(name):
            return ctx.enter_context(nc.semaphore(name))

        def sb(name, shape, dt=F32):
            return ctx.enter_context(nc.sbuf_tensor(name, shape, dt))

        stage = sb("stage", [P, STAGES, LOT, HALF_W])
        w_hi = sb("w_hi", [P, RING, HALF_W], F32R)
        w_lo = sb("w_lo", [P, RING, HALF_W], F32R)
        ident = sb("ident", [P, P])
        ident_b = sb("ident_b", [P, P], BF16)
        hide_b = sb("hide_b", [P, P], BF16)
        rows = FOX_HEADS + ML_HEADS
        pick = sb("pick", [P, rows, P], F32R)
        decay = sb("decay", [P, P * NT * (NT + 1) // 2], F32R)
        n_param = CONV_K * KT + KT + 2 * KT + ML_HEADS
        param_rows = sb("param_rows", [n_param, P])
        param = sb("param", [P, n_param])
        conv_taps = param[:, 0:CONV_K * KT].rearrange("p (j c) -> p c j", j=CONV_K)
        conv_bias = param[:, CONV_K * KT:CONV_K * KT + KT]
        gate_bias = param[:, CONV_K * KT + KT:CONV_K * KT + 3 * KT]
        ml_gain = param[:, CONV_K * KT + 3 * KT:n_param]
        bias16 = sb("bias16", [P, 16])
        gate16 = sb("gate16", [P, NT, 16])
        soft16 = sb("soft16", [P, 3, NT, rows])
        forget = sb("forget", [P, NT, rows])
        enter = sb("enter", [P, NT, rows])
        c_tile = sb("c_tile", [P, NT, rows])
        c_all = sb("c_all", [P, NT, rows])
        stat = sb("stat", [P, 2, 8])
        peak = sb("peak", [P, 2])
        total = sb("total", [P, 2])
        inv = sb("inv", [P, 2])
        ml_m = sb("ml_m", [P, 2, 4])
        ml_top = sb("ml_top", [P, ML_HEADS, NT])
        ml_den = sb("ml_den", [P, ML_HEADS, NT])
        ml_stat = sb("ml_stat", [P, 10, NT])

        a0 = nc.sbuf_base

        def at(name, kb, shape, dt=F32):
            return nc.alloc_sbuf_tensor_at(name, shape, dt, offset=a0 + int(kb * KB))

        A1 = 96
        act1_hi, act1_lo = at("act1_hi", A1, [P, KT, TOK], F32R), at("act1_lo", A1 + 16, [P, KT, TOK], F32R)
        fox_q, fox_k, fox_v = (at(n, 8 * i, [P, 4, TOK]) for i, n in enumerate(("fox_q", "fox_k", "fox_v")))
        ml_q, ml_k, ml_v = (at(n, 24 + 8 * i, [P, 4, TOK]) for i, n in enumerate(("ml_q", "ml_k", "ml_v")))
        yf_hi, yf_lo = at("yf_hi", 0, [P, 4, TOK], F32R), at("yf_lo", 8, [P, 4, TOK], F32R)
        ym_hi, ym_lo = at("ym_hi", 24, [P, 4, TOK], F32R), at("ym_lo", 32, [P, 4, TOK], F32R)
        prob = at("prob", 48, [P, 2, TOK])
        prob_t = at("prob_t", 52, [P, 2, TOK])
        dwt = at("dwt", 56, [P, TOK])
        conv_u = at("conv_u", 58, [P, 2, TOK + 16])
        conv_acc = at("conv_acc", 62.25, [P, 2, TOK])
        conv_th = at("conv_th", 66.25, [P, 2, TOK])
        gate_rows = at("gate_rows", 66.25, [16, TOK])
        gate_m = at("gate_m", 58, [P, 4, TOK])
        ml_h = at("ml_h", 66.25, [P, ML_HD * NT])
        ml_h2 = at("ml_h2", 68.25, [P, ML_HD * NT])
        gate_f = at("gate_f", 70.5, [P, KT, TOK])
        ml_th = at("ml_th", 86.5, [P, 4, TOK])
        w16 = at("w16", 94.5, [P, KT, 16])
        w16_hi, w16_lo = at("w16_hi", 95, [P, KT, 16], F32R), at("w16_lo", 95.5, [P, KT, 16], F32R)
        upto = at("upto", 84, [P, P])
        beyond = at("beyond", 84.5, [P, P])
        minus1 = at("minus1", 85, [P, P])
        ones = at("ones", 85.5, [P, P])
        x_tok = at("x_tok", 24, [P, NT, DM])
        scaled = at("scaled", 72, [P, 2, DM])
        row_a = at("row_a", 80, [P, DM])
        row_b = at("row_b", 92, [P, DM])
        act2_hi, act2_lo = at("act2_hi", 0, [P, KT, TOK], F32R), at("act2_lo", 16, [P, KT, TOK], F32R)
        mem_k = at("mem_k", 32, [P, KT, MEM])
        h_tok = at("h_tok", 40, [P, NT, DM])
        mem_hi, mem_lo = at("mem_hi", 56, [P, KT, MEM], F32R), at("mem_lo", 64, [P, KT, MEM], F32R)
        mem_v = at("mem_v", 84, [P, MEM // P, DM])
        mem_tok = at("mem_tok", 86.5, [P, MEM // P, DM])
        x_prob = at("x_prob", 72, [P, 2, MEM])
        x_q = at("x_q", A1, [P, KT, TOK])
        x_prob_t = at("x_prob_t", A1 + 16, [P, X_HEADS, MEM // P, TOK])
        relu = at("relu", 56, [P, 2, TOK])
        relu2 = at("relu2", 60, [P, 2, TOK])
        result = at("result", 72, [P, 2, DM])

        bank = [ctx.enter_context(nc.psum_tensor(f"bank{i}", [P, 512], F32)) for i in range(8)]

        s_xt = [sem(f"s_x{i}") for i in range(NT)]
        s_small = sem("s_small")
        s_const = sem("s_const")
        s_mem = sem("s_mem")
        s_residual = sem("s_residual")
        s_row_x, s_row_a, s_row_b = sem("s_row_x"), sem("s_row_a"), sem("s_row_b")
        s_param, s_pturned = sem("s_param"), sem("s_pturned")
        s_lot = [sem(f"s_lot{i}") for i in range(STAGES)]
        s_high = sem("s_high")
        s_low = sem("s_low")
        s_half = sem("s_half")
        s_taken = [sem("s_taken0"), sem("s_taken1")]
        s_squares, s_scaled, s_nturn = sem("s_squares"), sem("s_scaled"), sem("s_nturn")
        s_nhigh, s_nlow = sem("s_nhigh"), sem("s_nlow")
        s_w16 = sem("s_w16")
        s_grows, s_gturn = sem("s_grows"), sem("s_gturn")
        s_gate = sem("s_gate")
        s_gabs, s_gexp, s_gln, s_forget = sem("s_gabs"), sem("s_gexp"), sem("s_gln"), sem("s_forget")
        s_rows, s_dhigh, s_dlow, s_sums = sem("s_rows"), sem("s_dhigh"), sem("s_dlow"), sem("s_sums")
        s_score, s_peak, s_exp, s_prob = sem("s_score"), sem("s_peak"), sem("s_exp"), sem("s_prob")
        s_pturn, s_pt, s_value = sem("s_pturn"), sem("s_pt"), sem("s_value")
        s_yfh, s_yfl = sem("s_yfh"), sem("s_yfl")
        s_emt, s_hm = sem("s_emt"), sem("s_hm")
        s_numer = sem("s_numer")
        s_mturn, s_mgate, s_ymh, s_yml = sem("s_mturn"), sem("s_mgate"), sem("s_ymh"), sem("s_yml")
        s_conv_u = sem("s_conv_u")
        s_acc, s_tanh, s_silu = sem("s_acc"), sem("s_tanh"), sem("s_silu")
        s_merged, s_merh, s_merl = sem("s_merged"), sem("s_merh"), sem("s_merl")
        s_xv, s_oh, s_ol = sem("s_xv"), sem("s_oh"), sem("s_ol")
        s_relu, s_relu2, s_ah, s_al = sem("s_relu"), sem("s_relu2"), sem("s_ah"), sem("s_al")
        s_result = sem("s_result")
        s_out = [sem("s_out0"), sem("s_out1")]
        s_chain = sem("s_chain")
        s_prep = sem("s_prep")

        block = ctx.enter_context(nc.Block())

        def taken(eng, g):
            eng.wait_ge(s_taken[g % 2], g // 2 + 1)

        def group_done(eng, g):
            n = max(i for i in range(len(UNITS)) if GROUP0[i] <= g)
            eng.wait_ge(s_half, group_end(n, g - GROUP0[n]))

        def unit_done(eng, name):
            n = UNIT[name]
            eng.wait_ge(s_half, group_end(n, UNITS[n][5] - 1))

        def task(t):
            h, i = (t // NT, t % NT) if t < ML0 else ((t - ML0) // NT, t % NT)
            return h, i, P * (i + 1)

        def x_bank(h, d):
            return bank[(6 if h < X_HEADS - 1 else 2) + d]

        def decay_at(i):
            return P * i * (i + 1) // 2

        n_norm = 3 * NT + 2

        def norm_source(n):
            if n < NT:
                return x_tok[:, n, :]
            if n < NT + 2:
                return mem_tok[:, n - NT, :]
            return h_tok[:, (n - NT - 2) % NT, :]

        def norm_gains(n):
            return ((row_a, s_row_x, 1), (row_a, s_row_a, 1), (row_b, s_row_b, 1), (row_a, s_row_a, 2),
                    (row_b, s_row_b, 2))[0 if n < NT else 1 if n < NT + 2 else 2 + (n - NT - 2) // NT]

        def norm_target(n, b):
            ks = slice(4 * b, 4 * b + 4)
            if n < NT:
                return act1_hi[:, ks, P * n:P * n + P], act1_lo[:, ks, P * n:P * n + P]
            if n < NT + 2:
                i = n - NT
                return mem_hi[:, ks, P * i:P * i + P], mem_lo[:, ks, P * i:P * i + P]
            i = (n - NT - 2) % NT
            if n < 2 * NT + 2:
                return act2_hi[:, ks, P * i:P * i + P], act2_lo[:, ks, P * i:P * i + P]
            return act1_hi[:, ks, P * i:P * i + P], act1_lo[:, ks, P * i:P * i + P]

        @block.sync
        def _(sp):
            def load_x(i):
                sp.dma_start(x_tok[:, i, :], x[P * i:P * i + P, :]).then_inc(s_xt[i], 16)

            load_x(0)
            sp.dma_start(row_a[:], norm_mix.partition_broadcast(P)).then_inc(s_row_x, 16)
            lot = 0
            for name, w, row0, nk, col0, _ in UNITS:
                src = weights[w][row0:row0 + nk * P, col0:col0 + HALF_W].rearrange("(k p) n -> p k n", p=P)
                for c in range(nk // LOT):
                    if lot >= STAGES:
                        sp.wait_ge(s_low, 2 * (lot - STAGES + 1))
                    sp.dma_start(stage[:, lot % STAGES, :, :], src[:, LOT * c:LOT * c + LOT, :])\
                      .then_inc(s_lot[lot % STAGES], 16)
                    lot += 1
                    if lot == 1:
                        load_x(1)
                    if lot == 2:
                        load_x(2)
                        load_x(3)
                        row = 0
                        for v in (conv_w.rearrange("j (c p) -> (j c) p", p=P), conv_b.rearrange("(c p) -> c p", p=P),
                                  b_gate.rearrange("(c p) -> c p", p=P), mlstm_norm.rearrange("(c p) -> c p", p=P)):
                            sp.dma_start(param_rows[row:row + v.shape[0], :], v).then_inc(s_param, 16)
                            row += v.shape[0]
            for i in range(NT):
                sp.wait_ge(s_result, i + 1)
                sp.dma_start(out[P * i:P * i + P, :], result[:, i % 2, :]).then_inc(s_out[i % 2], 16)
            for s in s_out:
                sp.wait_ge(s, 16 * NT // 2)

        @block.gpsimd
        def _(pool):
            n = 0

            def fill(ins):
                nonlocal n
                ins.then_inc(s_const, 1)
                n += 1

            fill(pool.memset(ones[:], 1.0))
            fill(pool.memset(ident[:], 0.0))
            fill(pool.memset(ident_b[:], 0.0))
            fill(pool.memset(hide_b[:], 0.0))
            fill(pool.memset(upto[:], 1.0))
            fill(pool.memset(beyond[:], -1.0))
            fill(pool.memset(minus1[:], -1.0))
            fill(pool.memset(pick[:].bitcast(F32), 0.0))
            fill(pool.memset(decay[:].bitcast(F32), 0.0))
            fill(pool.memset(conv_u[:], 0.0))
            fill(pool.memset(enter[:], 0.0))
            pool.wait_ge(s_const, n)
            for m in (ident, ident_b):
                fill(pool.affine_select(out=m[:], in_=m[:], compare_op=ALU.not_equal, fill=1.0, base=0,
                                        pattern=[[-1, P]], channel_multiplier=1))
            fill(pool.affine_select(out=hide_b[:], in_=hide_b[:], compare_op=ALU.is_ge, fill=HIDE, base=0,
                                    pattern=[[-1, P]], channel_multiplier=1))
            fill(pool.affine_select(out=upto[:], in_=upto[:], compare_op=ALU.is_ge, fill=0.0, base=0,
                                    pattern=[[1, P]], channel_multiplier=-1))
            fill(pool.affine_select(out=beyond[:], in_=beyond[:], compare_op=ALU.is_gt, fill=0.0, base=0,
                                    pattern=[[-1, P]], channel_multiplier=1))
            for r in (0, 32):
                pool.wait_ge(s_const, n)
                fill(pool.affine_select(out=pick[:], in_=pick[:].bitcast(F32), compare_op=ALU.not_equal, fill=1.0,
                                        base=-r, pattern=[[-1, rows], [0, P]], channel_multiplier=1))
            assert n == N_CONST
            n_small = 0

            def small(dst, src):
                nonlocal n_small
                with nc.allow_non_contiguous_dma(reason="small parameters"):
                    pool.dma_start(dst, src, allow_slow_non_contiguous=True).then_inc(s_small, 16)
                n_small += 1

            small(w16[:, :, 0:8], w_in[:, C_FF:C_FF + 8].rearrange("(k p) n -> p k n", p=P))
            small(w16[:, :, 8:12], w_in[:, C_MI + 4:C_MI + 8].rearrange("(k p) n -> p k n", p=P))
            small(w16[:, :, 12:16], w_in[:, C_MI:C_MI + 4].rearrange("(k p) n -> p k n", p=P))
            small(bias16[:, 0:8], b_fox_f.partition_broadcast(P))
            small(bias16[:, 8:12], b_mlstm_f.partition_broadcast(P))
            small(bias16[:, 12:16], b_mlstm_i.partition_broadcast(P))
            assert n_small == N_SMALL
            pool.wait_ge(s_value, X0)
            pool.wait_ge(s_hm, ML_HEADS)
            pool.dma_start(h_tok[:], x.rearrange("(i p) n -> p i n", p=P)).then_inc(s_residual, 16)
            pool.wait_ge(s_yml, ML_HEADS)
            pool.dma_start(mem_tok[:], mem.rearrange("(i p) n -> p i n", p=P)).then_inc(s_mem, 16)
            pool.wait_ge(s_merl, KT)

            def load_row(row, gains, s):
                pool.dma_start(row[:], gains.partition_broadcast(P)).then_inc(s, 16)

            load_row(row_a, norm_mem, s_row_a)
            pool.wait_ge(s_scaled, NT + 2)
            load_row(row_b, norm_xattn, s_row_b)
            load_row(row_a, norm_mlp, s_row_a)
            pool.wait_ge(s_scaled, 2 * NT + 2)
            load_row(row_b, norm_final, s_row_b)

        @block.scalar
        def _(act):
            def copy(dst, src, **k):
                return act.activation(dst, src, ACT.Copy, **k)

            def high_weights(pair):
                lot = pair // 2
                act.wait_ge(s_lot[lot % STAGES], 16 * (lot // STAGES + 1))
                f = free_after(pair)
                if f >= 0:
                    act.wait_ge(s_half, f + 1)
                r = (2 * pair) % RING
                copy(w_hi[:, r:r + 2, :], stage[:, lot % STAGES, 2 * (pair % 2):2 * (pair % 2) + 2, :])\
                    .then_inc(s_high, 1)

            def take(g):
                n = max(i for i in range(len(UNITS)) if GROUP0[i] <= g)
                j, k, b = g - GROUP0[n], kind(n), bank[g % 2]
                free = s_taken[g % 2]
                if k in ("fox_q", "up_fox", "up_ml", "mix", "x_out", "mlp_out"):
                    return
                group_done(act, g)
                if k == "fox_k":
                    copy(fox_k[:, j, :], b[:]).then_inc(free, 1)
                elif k == "fox_v":
                    copy(fox_v[:, j, :], b[:]).then_inc(free, 1)
                elif k == "ml_v":
                    copy(ml_v[:, j, :], b[:]).then_inc(free, 1)
                elif k in ("conv_q", "conv_k"):
                    c = j + (4 if k == "conv_k" else 0)
                    if c == 0:
                        act.wait_ge(s_const, N_CONST)
                    if c >= 2:
                        act.wait_ge(s_acc, c - 1)
                    copy(conv_u[:, c % 2, 3:3 + TOK], b[:]).then_inc(s_conv_u, 1)
                    if c >= 2:
                        act.wait_ge(s_silu, c - 1)
                    act.wait_ge(s_prep, 1)
                    act.activation(conv_acc[:, c % 2, :], b[:], ACT.Identity, scale=conv_taps[:, c, 3:4],
                                   bias=conv_bias[:, c:c + 1]).then_inc(free, 1)
                elif k == "ml_o":
                    act.activation(ml_th[:, j, :], b[:], ACT.Tanh, scale=0.5).then_inc(free, 1)
                elif k in ("gate_fox", "gate_ml"):
                    t = 4 * order(n) + j
                    dst = gate_f[:, t, :] if k == "gate_fox" else gate_m[:, j, :]
                    if k == "gate_ml" and order(n) == 1:
                        act.wait_ge(s_merged, 4)
                    if k == "gate_ml" and order(n) == 0:
                        act.wait_ge(s_silu, 2 * 4)
                    col = t + (KT if k == "gate_ml" else 0)
                    act.wait_ge(s_prep, 1)
                    act.activation(dst, b[:], ACT.Tanh, scale=0.5, bias=gate_bias[:, col:col + 1]).then_inc(free, 1)
                elif k == "mem_k":
                    copy(mem_k[:, 4 * order(n) + j, :], b[:, 0:MEM]).then_inc(free, 1)
                elif k == "x_q":
                    act.activation(x_q[:, 4 * order(n) + j, :], b[:], ACT.Copy, scale=X_HD ** -0.5).then_inc(free, 1)
                elif k == "mem_v":
                    copy(mem_v[:, j, HALF_W * order(n):HALF_W * (order(n) + 1)], b[:]).then_inc(free, 1)
                elif k == "mlp_in":
                    a = 4 * order(n) + j
                    if a >= 2:
                        act.wait_ge(s_relu2, a - 1)
                    act.activation(relu[:, a % 2, :], b[:], ACT.Relu).then_inc(free, 1)
                    act.wait_ge(s_relu2, a + 1)
                    copy(act2_hi[:, a % KT, :], relu2[:, a % 2, :]).then_inc(s_ah, 1)

            def norm(n):
                if n < NT:
                    act.wait_ge(s_xt[n], 16)
                elif n < NT + 2:
                    act.wait_ge(s_mem, 16)
                else:
                    i = (n - NT - 2) % NT
                    u = ("mix1", "x_out1", f"mlp_out{2 * FF // DM - 1}")[(n - NT - 2) // NT]
                    taken(act, GROUP0[UNIT[u]] + i)
                if 2 <= n < n_norm + 2:
                    act.wait_ge(s_scaled, n - 1 if n < n_norm else n_norm)
                if 2 <= n < n_norm:
                    act.wait_ge(s_nturn, 2 * (n - 1))
                if n >= n_norm:
                    act.wait_ge(s_nturn, 2 * n_norm)
                if n >= n_norm + 2:
                    act.wait_ge(s_out[n % 2], 16 * ((n - n_norm) // 2))
                act.activation(scaled[:, n % 2, :], norm_source(n), ACT.Square, accum_out=stat[:, n % 2, 0:1])\
                    .then_inc(s_squares, 1)

            for step, n in steps:
                if step == "split_weights":
                    high_weights(n)
                elif step == "take":
                    take(n)
                elif step == "norm":
                    norm(n)
                elif step == "norm_split":
                    for b in range(2):
                        act.wait_ge(s_nturn, 2 * n + b + 1)
                        copy(norm_target(n, b)[0],
                             bank[2 + 2 * (n % 2) + b][:].rearrange("p (k t) -> p k t", k=4)).then_inc(s_nhigh, 1)
                elif step == "conv_tanh":
                    act.wait_ge(s_acc, n + 1)
                    act.activation(conv_th[:, n % 2, :], conv_acc[:, n % 2, :], ACT.Tanh).then_inc(s_tanh, 1)
                elif step == "gate_rows":
                    act.wait_ge(s_gate, 1)
                    copy(gate_rows[:], bank[6][0:16, :]).then_inc(s_grows, 1)
                elif step == "gate_turn":
                    act.wait_ge(s_gabs, 1)
                    act.activation(soft16[:, 1], soft16[:, 0], ACT.Exp, scale=-1.0).then_inc(s_gexp, 1)
                    act.wait_ge(s_gexp, 1)
                    act.activation(soft16[:, 2], soft16[:, 1], ACT.Ln, bias=1.0).then_inc(s_gln, 1)
                elif step == "decay":
                    for i in range(NT):
                        act.wait_ge(s_rows, i + 1)
                        copy(decay[0:rows, decay_at(i):decay_at(i + 1)], bank[2 + i][0:rows, 0:P * (i + 1)])\
                            .then_inc(s_dhigh, 1)
                elif step == "probs" and n < ML0:
                    _, _, keys = task(n)
                    act.wait_ge(s_peak, n + 1)
                    if n >= 2:
                        act.wait_ge(s_pturn, n - 1)
                    act.activation(prob[:, n % 2, 0:keys], bank[2 + n % 2][:, 0:keys], ACT.Exp,
                                   bias=peak[:, n % 2:n % 2 + 1], accum_out=total[:, n % 2:n % 2 + 1])\
                        .then_inc(s_exp, 1)
                elif step == "probs" and n < X0:
                    _, _, keys = task(n)
                    act.wait_ge(s_peak, n + 1)
                    act.wait_ge(s_prob, n)
                    act.activation(dwt[:, 0:keys], bank[2 + n % 2][:, 0:keys], ACT.Exp,
                                   bias=ml_m[:, n % 2, 1:2]).then_inc(s_exp, 1)
                elif step == "probs":
                    act.wait_ge(s_peak, n + 1)
                    if n - X0 >= 2:
                        act.wait_ge(s_pturn, n - 1)
                    act.activation(x_prob[:, n % 2, :], bank[2 + n % 2][:, 0:MEM], ACT.Exp,
                                   bias=peak[:, n % 2:n % 2 + 1], accum_out=total[:, n % 2:n % 2 + 1])\
                        .then_inc(s_exp, 1)
                elif step == "turned" and n < X0:
                    _, _, keys = task(n)
                    act.wait_ge(s_pturn, n + 1)
                    if n >= 2:
                        act.wait_ge(s_value, n - 1)
                    src = bank[4 + n % 2] if n < ML0 else bank[4]
                    copy(prob_t[:, n % 2, 0:keys], src[:, 0:keys]).then_inc(s_pt, 1)
                elif step == "turned":
                    h, i = (n - X0) // NT, n % NT
                    act.wait_ge(s_pturn, n + 1)
                    copy(x_prob_t[:, h, :, P * i:P * i + P],
                         bank[4 + n % 2][:, 0:MEM].rearrange("p (k t) -> p k t", k=2)).then_inc(s_pt, 1)
                elif step == "fox_split":
                    act.wait_ge(s_value, 2 * NT * (n + 1))
                    copy(yf_hi[:, n, :], bank[6 + n % 2][:]).then_inc(s_yfh, 1)
                elif step == "ml_quotient":
                    act.wait_ge(s_prob, ML0 + NT * (n + 1))
                    if n > 0:
                        act.wait_ge(s_hm, n)
                    act.activation(ml_stat[:, 0, :], ml_top[:, n, :], ACT.Exp, scale=-1.0).then_inc(s_emt, 1)
                elif step == "ml_split":
                    act.wait_ge(s_mgate, n + 1)
                    act.activation(ym_hi[:, n, :], ml_h2[:], ACT.Copy, scale=ml_gain[:, n:n + 1]).then_inc(s_ymh, 1)
                elif step == "merge_split":
                    if n == 0:
                        unit_done(act, "gate_ml1")
                    act.wait_ge(s_merged, n + 1)
                    act.activation(act1_hi[:, n, :], gate_f[:, n, :], ACT.Copy, scale=0.5).then_inc(s_merh, 1)
                elif step == "x_split":
                    for d in range(2):
                        act.wait_ge(s_xv, 2 * n + d + 1)
                        copy(act2_hi[:, 2 * n + d, :], x_bank(n, d)[:]).then_inc(s_oh, 1)

        @block.vector
        def _(dve):
            links = [0]

            def link(ins):
                links[0] += 1
                ins.then_inc(s_chain, 1)
                dve.wait_ge(s_chain, links[0])

            def inverse_root(dst, val, half, tmp):
                link(dve.tensor_scalar(tmp.bitcast(I32), val.bitcast(I32), 1, None, ALU.arith_shift_right))
                link(dve.tensor_scalar(dst.bitcast(I32), tmp.bitcast(I32), -1.0, float(0x5F3759DF), ALU.mult, ALU.add))
                for _ in range(3):
                    if dst.shape[1] == 1:
                        link(dve.scalar_tensor_tensor(tmp, dst, half, dst, ALU.mult, ALU.mult))
                    else:
                        link(dve.tensor_tensor(tmp, dst, dst, ALU.mult))
                        link(dve.tensor_tensor(tmp, tmp, half, ALU.mult))
                    link(dve.scalar_tensor_tensor(dst, tmp, 1.5, dst, ALU.add, ALU.mult))

            def mean_square(val, half, squares, width):
                link(dve.tensor_scalar(val, squares, 1.0 / width, EPS, ALU.mult, ALU.add))
                link(dve.tensor_scalar(half, squares, -0.5 / width, -0.5 * EPS, ALU.mult, ALU.add))

            def low_weights(pair):
                dve.wait_ge(s_high, pair + 1)
                lot, r = pair // 2, (2 * pair) % RING
                src = stage[:, lot % STAGES, 2 * (pair % 2):2 * (pair % 2) + 2, :]
                dve.tensor_tensor(w_lo[:, r:r + 2, :], src, w_hi[:, r:r + 2, :].bitcast(F32), ALU.subtract)\
                   .then_inc(s_low, 1)

            def take(g):
                n = max(i for i in range(len(UNITS)) if GROUP0[i] <= g)
                j, k, b = g - GROUP0[n], kind(n), bank[g % 2]
                free = s_taken[g % 2]
                if k == "fox_q":
                    group_done(dve, g)
                    dve.tensor_scalar(fox_q[:, j, :], b[:], FOX_HD ** -0.5, None, ALU.mult).then_inc(free, 1)
                elif k in ("conv_q", "conv_k"):
                    c = j + (4 if k == "conv_k" else 0)
                    u, acc = conv_u[:, c % 2, :], conv_acc[:, c % 2, :]
                    taken(dve, g)
                    for q in range(CONV_K - 1):
                        ins = dve.scalar_tensor_tensor(acc, u[:, q:q + TOK], conv_taps[:, c, q:q + 1], acc,
                                                       ALU.mult, ALU.add)
                        if q < CONV_K - 2:
                            link(ins)
                    ins.then_inc(s_acc, 1)
                elif k == "up_fox":
                    group_done(dve, g)
                    t = 4 * order(n) + j
                    taken(dve, GROUP0[UNIT[f"gate_fox{order(n)}"]] + j)
                    dve.scalar_tensor_tensor(gate_f[:, t, :], gate_f[:, t, :], 1.0, b[:], ALU.add, ALU.mult)\
                       .then_inc(free, 1)
                elif k == "up_ml":
                    group_done(dve, g)
                    t = 4 * order(n) + j
                    taken(dve, GROUP0[UNIT[f"gate_ml{order(n)}"]] + j)
                    dve.scalar_tensor_tensor(gate_m[:, j, :], gate_m[:, j, :], 1.0, b[:], ALU.add, ALU.mult)\
                       .then_inc(free, 1)
                    taken(dve, g)
                    taken(dve, GROUP0[UNIT[f"up_fox{order(n)}"]] + j)
                    dve.tensor_tensor(gate_f[:, t, :], gate_f[:, t, :], gate_m[:, j, :], ALU.add)\
                       .then_inc(s_merged, 1)
                elif k in ("mix", "x_out", "mlp_out"):
                    group_done(dve, g)
                    c = order(n) % 2
                    if k == "mix":
                        dve.wait_ge(s_residual, 16)
                    elif k == "x_out":
                        taken(dve, GROUP0[UNIT[f"mix{c}"]] + j)
                    elif order(n) < 2:
                        taken(dve, GROUP0[UNIT[f"x_out{c}"]] + j)
                    else:
                        taken(dve, GROUP0[UNIT[f"mlp_out{order(n) - 2}"]] + j)
                    dst = h_tok[:, j, HALF_W * c:HALF_W * (c + 1)]
                    dve.tensor_tensor(dst, b[:], dst, ALU.add).then_inc(free, 1)
                elif k == "mlp_in":
                    a = 4 * order(n) + j
                    taken(dve, g)
                    if a >= 2:
                        dve.wait_ge(s_al, a - 1)
                    dve.tensor_tensor(relu2[:, a % 2, :], relu[:, a % 2, :], relu[:, a % 2, :], ALU.mult)\
                       .then_inc(s_relu2, 1)
                    dve.wait_ge(s_ah, a + 1)
                    dve.tensor_tensor(act2_lo[:, a % KT, :], relu2[:, a % 2, :],
                                      act2_hi[:, a % KT, :].bitcast(F32), ALU.subtract).then_inc(s_al, 1)

            def silu(c):
                dst = ml_q[:, c, :] if c < 4 else ml_k[:, c - 4, :]
                dve.wait_ge(s_tanh, c + 1)
                dve.scalar_tensor_tensor(dst, conv_th[:, c % 2, :], 1.0, conv_acc[:, c % 2, :], ALU.add, ALU.mult)\
                   .then_inc(s_silu, 1)

            def norm(n):
                st = stat[:, n % 2, :]
                dve.wait_ge(s_squares, n + 1)
                mean_square(st[:, 1:2], st[:, 3:4], st[:, 0:1], DM)
                inverse_root(st[:, 2:3], st[:, 1:2], st[:, 3:4], st[:, 4:5])
                row, s_row, loads = norm_gains(n)
                dve.wait_ge(s_row, 16 * loads)
                dst, done = (scaled, s_scaled) if n < n_norm else (result, s_result)
                dve.scalar_tensor_tensor(dst[:, n % 2, :], norm_source(n), st[:, 2:3], row[:],
                                         ALU.mult, ALU.mult).then_inc(done, 1)

            h3, g3 = (v[:].rearrange("p (i e) -> p i e", i=NT) for v in (ml_h, ml_h2))
            for step, n in steps:
                if step == "split_weights":
                    low_weights(n)
                elif step == "take":
                    take(n)
                elif step == "norm":
                    norm(n)
                elif step == "norm_split":
                    for b in range(2):
                        hi, lo = norm_target(n, b)
                        dve.wait_ge(s_nhigh, 2 * n + b + 1)
                        src = bank[2 + 2 * (n % 2) + b][:].rearrange("p (k t) -> p k t", k=4)
                        dve.tensor_tensor(lo, src, hi.bitcast(F32), ALU.subtract).then_inc(s_nlow, 1)
                elif step == "parameters":
                    dve.wait_ge(s_pturned, 1)
                    dve.tensor_scalar(param[:], bank[6][:, 0:n_param], 0.5, None, ALU.mult).then_inc(s_prep, 1)
                    dve.wait_ge(s_small, 16 * N_SMALL)
                    link(dve.tensor_copy(w16_hi[:], w16[:]))
                    dve.tensor_tensor(w16_lo[:], w16[:], w16_hi[:].bitcast(F32), ALU.subtract).then_inc(s_w16, 1)
                elif step == "conv_silu":
                    silu(n)
                elif step == "gate_turn":
                    dve.wait_ge(s_gturn, 1)
                    b16 = bias16[:].unsqueeze(1).to_broadcast([P, NT, 16])
                    link(dve.tensor_tensor(gate16[:], bank[7][:, 0:16 * NT].rearrange("p (i g) -> p i g", g=16),
                                           b16, ALU.add))
                    f = gate16[:, :, 0:rows]
                    dve.scalar_tensor_tensor(soft16[:, 0], f, -1.0, f, ALU.mult, ALU.max).then_inc(s_gabs, 1)
                    dve.wait_ge(s_gln, 1)
                    link(dve.tensor_scalar(soft16[:, 1], f, -1.0, 0.0, ALU.mult, ALU.max))
                    link(dve.tensor_tensor(forget[:], soft16[:, 1], soft16[:, 2], ALU.add))
                    dve.wait_ge(s_const, N_CONST)
                    dve.tensor_copy(enter[:, :, FOX_HEADS:rows], gate16[:, :, rows:16]).then_inc(s_forget, 1)
                elif step == "decay":
                    for i in range(NT):
                        dve.wait_ge(s_dhigh, i + 1)
                        dve.tensor_tensor(decay[32:32 + rows, decay_at(i):decay_at(i + 1)],
                                          bank[2 + i][0:rows, 0:P * (i + 1)],
                                          decay[0:rows, decay_at(i):decay_at(i + 1)].bitcast(F32),
                                          ALU.subtract).then_inc(s_dlow, 1)
                    dve.wait_ge(s_sums, 1)
                    link(dve.tensor_scalar(c_tile[:], bank[6][:, 0:NT * rows].rearrange("p (i g) -> p i g", i=NT),
                                           -1.0, None, ALU.mult))
                    link(dve.tensor_scalar(c_all[:], bank[6][:, 64:64 + NT * rows].rearrange("p (i g) -> p i g", i=NT),
                                           -1.0, None, ALU.mult))
                elif step == "probs" and (n < ML0 or n >= X0):
                    keys = task(n)[2] if n < ML0 else MEM
                    i2 = n % 2
                    dve.wait_ge(s_score, n + 1)
                    dve.tensor_reduce(peak[:, i2:i2 + 1], bank[2 + i2][:, 0:keys], AX_X, ALU.max, negate=True)\
                       .then_inc(s_peak, 1)
                    dve.wait_ge(s_exp, n + 1)
                    link(dve.reciprocal(inv[:, i2:i2 + 1], total[:, i2:i2 + 1]))
                    p = prob[:, i2, 0:keys] if n < ML0 else x_prob[:, i2, :]
                    dve.tensor_scalar(p, p, inv[:, i2:i2 + 1], None, ALU.mult).then_inc(s_prob, 1)
                elif step == "probs":
                    h, i, keys = task(n)
                    i2, row = n % 2, FOX_HEADS + task(n)[0]
                    dve.wait_ge(s_score, n + 1)
                    link(dve.tensor_reduce(ml_m[:, i2, 0:1], bank[2 + i2][:, 0:keys], AX_X, ALU.max))
                    link(dve.scalar_tensor_tensor(ml_top[:, h, i:i + 1], ml_m[:, i2, 0:1], c_tile[:, i, row:row + 1],
                                                  c_all[:, i, row:row + 1], ALU.add, ALU.max))
                    dve.tensor_tensor(ml_m[:, i2, 1:2], c_tile[:, i, row:row + 1], ml_top[:, h, i:i + 1],
                                      ALU.subtract).then_inc(s_peak, 1)
                    dve.wait_ge(s_exp, n + 1)
                    dve.wait_ge(s_pturn, n - 1)
                    dve.tensor_tensor_reduce(prob[:, i2, 0:keys], bank[5][:, 0:keys], dwt[:, 0:keys],
                                             ML_HD ** -0.5, 0.0, ALU.mult, ALU.add,
                                             ml_den[:, h, i:i + 1]).then_inc(s_prob, 1)
                elif step == "fox_split":
                    dve.wait_ge(s_yfh, n + 1)
                    dve.tensor_tensor(yf_lo[:, n, :], bank[6 + n % 2][:], yf_hi[:, n, :].bitcast(F32), ALU.subtract)\
                       .then_inc(s_yfl, 1)
                elif step == "ml_quotient":
                    num = bank[6 + n % 2][:].rearrange("p (i e) -> p i e", i=NT)
                    dve.wait_ge(s_prob, ML0 + NT * (n + 1))
                    dve.wait_ge(s_emt, n + 1)
                    link(dve.scalar_tensor_tensor(ml_stat[:, 1, :], ml_den[:, n, :], -1.0, ml_den[:, n, :],
                                                  ALU.mult, ALU.max))
                    link(dve.tensor_tensor(ml_stat[:, 2, :], ml_stat[:, 1, :], ml_stat[:, 0, :], ALU.max))
                    link(dve.reciprocal(ml_stat[:, 3, :], ml_stat[:, 2, :]))
                    dve.wait_ge(s_value, ML0 + NT * (n + 1))
                    if n > 0:
                        dve.wait_ge(s_mturn, n)
                    dve.tensor_tensor(h3, num, ml_stat[:, 3, :].unsqueeze(2).to_broadcast([P, NT, ML_HD]), ALU.mult)\
                       .then_inc(s_numer, 1)
                elif step == "ml_squares":
                    dve.wait_ge(s_numer, n + 1)
                    if n > 0:
                        dve.wait_ge(s_yml, n)
                    link(dve.tensor_tensor(g3, h3, h3, ALU.mult))
                    link(dve.tensor_reduce(ml_stat[:, 4, :], g3, AX_X, ALU.add))
                elif step == "ml_norm":
                    mean_square(ml_stat[:, 5, :], ml_stat[:, 7, :], ml_stat[:, 4, :], ML_HD)
                    inverse_root(ml_stat[:, 6, :], ml_stat[:, 5, :], ml_stat[:, 7, :], ml_stat[:, 8, :])
                    dve.tensor_tensor(h3, h3, ml_stat[:, 6, :].unsqueeze(2).to_broadcast([P, NT, ML_HD]), ALU.mult)\
                       .then_inc(s_hm, 1)
                elif step == "ml_split":
                    dve.wait_ge(s_mturn, n + 1)
                    dve.scalar_tensor_tensor(ml_h2[:], ml_th[:, n, :], 1.0, bank[6 + n % 2][:], ALU.add, ALU.mult)\
                       .then_inc(s_mgate, 1)
                    dve.wait_ge(s_ymh, n + 1)
                    dve.scalar_tensor_tensor(ym_lo[:, n, :], ml_h2[:], ml_gain[:, n:n + 1],
                                             ym_hi[:, n, :].bitcast(F32), ALU.mult, ALU.subtract).then_inc(s_yml, 1)
                elif step == "merge_split":
                    dve.wait_ge(s_merh, n + 1)
                    dve.scalar_tensor_tensor(act1_lo[:, n, :], gate_f[:, n, :], 0.5, act1_hi[:, n, :].bitcast(F32),
                                             ALU.mult, ALU.subtract).then_inc(s_merl, 1)
                elif step == "x_split":
                    for d in range(2):
                        dve.wait_ge(s_oh, 2 * n + d + 1)
                        dve.tensor_tensor(act2_lo[:, 2 * n + d, :], x_bank(n, d)[:],
                                          act2_hi[:, 2 * n + d, :].bitcast(F32), ALU.subtract).then_inc(s_ol, 1)

        @block.tensor
        def _(pe):
            sources = {
                "up_fox": (yf_hi, yf_lo), "up_ml": (ym_hi, ym_lo), "mix": (act1_hi, act1_lo),
                "mem_k": (mem_hi, mem_lo), "mem_v": (mem_hi, mem_lo), "x_q": (act2_hi, act2_lo),
                "x_out": (act2_hi, act2_lo), "mlp_in": (act1_hi, act1_lo), "mlp_out": (act2_hi, act2_lo),
            }

            def source_ready(n, k, end):
                name = kind(n)
                if name == "up_fox":
                    pe.wait_ge(s_yfl, k + 1)
                elif name == "up_ml":
                    pe.wait_ge(s_yml, k + 1)
                elif name == "mix":
                    pe.wait_ge(s_merl, k + 1)
                elif name == "x_out":
                    pe.wait_ge(s_ol, k + 1)
                elif name == "mlp_out":
                    pe.wait_ge(s_al, KT * (order(n) // 2) + k + 1)
                elif k % 4 == 0:
                    tiles = {"mem_k": NT + 2, "mem_v": NT + 2, "x_q": 2 * NT + 2, "mlp_in": n_norm}.get(name, NT)
                    if name == "mlp_in" and end < TOK:
                        tiles -= 1
                    pe.wait_ge(s_nlow, 2 * tiles - 1 + k // 4)

            def half(i):
                n, j, c, col, end = HALVES[i]
                nk, g, name = UNITS[n][3], GROUP0[n] + j, kind(n)
                hi, lo = sources.get(name, (act1_hi, act1_lo))
                if c == 0 and g >= 2:
                    taken(pe, g - 2)
                dst = bank[g % 2][:, col:end]
                for k in range(4 * c, 4 * c + 4):
                    slab = SLAB0[n] + k
                    r = slab % RING
                    if name == "fox_v":
                        pe.wait_ge(s_nlow, 2 * j + 1 + k // 4)
                    if j == 0:
                        if k % 2 == 0:
                            pe.wait_ge(s_low, slab // 2 + 1)
                        if name != "fox_v":
                            source_ready(n, k, end)
                    if by_tokens(n):
                        still = [(a[:, k, P * j:P * j + P]) for a in (hi, hi, lo)]
                        moving = [(w[:, r, :]) for w in (w_hi, w_lo, w_hi)]
                    else:
                        still = [(w[:, r, P * j:P * j + P]) for w in (w_hi, w_hi, w_lo)]
                        moving = [(a[:, k, col:end]) for a in (hi, lo, hi)]
                    for q in range(3):
                        ins = pe.matmul(dst, still[q], moving[q], start=(k == 0 and q == 0),
                                        stop=(k == nk - 1 and q == 2))
                ins.then_inc(s_half, 1)

            def norm_turn(n):
                pe.wait_ge(s_scaled, n + 1)
                if n == 0:
                    pe.wait_ge(s_const, N_CONST)
                if n >= 2:
                    pe.wait_ge(s_nlow, 2 * (n - 1))
                for b in range(2):
                    for q in range(4):
                        k = 4 * b + q
                        ins = pe.transpose(bank[2 + 2 * (n % 2) + b][:, P * q:P * q + P],
                                           scaled[:, n % 2, P * k:P * k + P], ident[:])
                    ins.then_inc(s_nturn, 1)

            def gates():
                pe.wait_ge(s_w16, 1)
                pe.wait_ge(s_nlow, 2 * NT)
                pe.wait_ge(s_prep, 1)
                for k in range(KT):
                    for q, (a, w) in enumerate(((act1_hi, w16_hi), (act1_hi, w16_lo), (act1_lo, w16_hi))):
                        ins = pe.matmul(bank[6][0:16, :], w[:, k, :], a[:, k, :],
                                        start=(k == 0 and q == 0), stop=(k == KT - 1 and q == 2))
                ins.then_inc(s_gate, 1)

            def decays():
                pe.wait_ge(s_forget, 1)
                for i in range(NT):
                    for j in range(i + 1):
                        dst = bank[2 + i][0:rows, P * j:P * j + P]
                        pe.matmul(dst, enter[:, j, :], ident[:], start=True, stop=False)
                        for u in range(j, max(i, j + 1)):
                            m = upto if j == i else beyond if u == j else minus1
                            ins = pe.matmul(dst, forget[:, u, :], m[:], start=False, stop=(u == max(i, j + 1) - 1))
                    ins.then_inc(s_rows, 1)
                for i in range(NT):
                    pe.matmul(bank[6][:, rows * i:rows * i + rows], upto[:], forget[:, i, :], start=True, stop=True)
                for i in range(NT):
                    for u in range(i + 1):
                        ins = pe.matmul(bank[6][:, 64 + rows * i:64 + rows * i + rows],
                                        (upto if u == i else ones)[:], forget[:, u, :],
                                        start=(u == 0), stop=(u == i))
                ins.then_inc(s_sums, 1)

            def scores(t):
                h, i, keys = task(t)
                if t == 0:
                    pe.wait_ge(s_dlow, NT)
                if t < ML0 and t % (2 * NT) == 0:
                    taken(pe, GROUP0[UNIT["fox_k"]] + h // 2)
                if t >= 2:
                    pe.wait_ge(s_exp, t - 1)
                s = bank[2 + t % 2]
                cols = slice(decay_at(i), decay_at(i) + keys)
                if t < ML0:
                    r = FOX_HD * (h % 2)
                    pe.matmul(s[:, 0:keys], fox_q[r:r + FOX_HD, h // 2, P * i:P * i + P],
                              fox_k[r:r + FOX_HD, h // 2, 0:keys], start=True, stop=False)
                    pe.matmul(s[:, 0:keys], pick[:, h, :], decay[:, cols], start=False, stop=False)
                else:
                    if t == ML0:
                        pe.wait_ge(s_silu, KT)
                        pe.wait_ge(s_pt, ML0)
                    pe.wait_ge(s_prob, t)
                    pe.matmul(bank[5][:, 0:keys], ml_q[:, h, P * i:P * i + P], ml_k[:, h, 0:keys],
                              start=True, stop=True)
                    pe.matmul(s[:, 0:keys], pick[:, FOX_HEADS + h, :], decay[:, cols], start=True, stop=False)
                pe.matmul(s[:, P * i:keys], ident_b[:], hide_b[:], start=False, stop=True).then_inc(s_score, 1)

            def x_scores(t):
                h, i = (t - X0) // NT, t % NT
                if h % 2 == 0 and i == 0:
                    n = UNIT[f"x_q{h // 2}"]
                    taken(pe, GROUP0[n] + 3)
                    taken(pe, GROUP0[n] + 2)
                    pe.wait_ge(s_nlow, 2 * (2 * NT + 2))
                pe.wait_ge(s_exp, t - 1)
                for d in range(2):
                    ins = pe.matmul(bank[2 + t % 2][:, 0:MEM], x_q[:, 2 * h + d, P * i:P * i + P],
                                    mem_k[:, 2 * h + d, :], start=(d == 0), stop=(d == 1))
                ins.then_inc(s_score, 1)

            def turn(t):
                pe.wait_ge(s_prob, t + 1)
                if t < X0:
                    keys, src = task(t)[2], prob[:, t % 2, :]
                    dst = bank[4 + t % 2] if t < ML0 else bank[4]
                    pe.wait_ge(s_pt, t if t >= ML0 else t - 1) if t >= 2 else None
                else:
                    keys, src, dst = MEM, x_prob[:, t % 2, :], bank[4 + t % 2]
                    pe.wait_ge(s_pt, t - 1)
                for j in range(keys // P):
                    ins = pe.transpose(dst[:, P * j:P * j + P], src[:, P * j:P * j + P], ident[:])
                ins.then_inc(s_pturn, 1)

            def values(t):
                h, i, _ = task(t)
                pe.wait_ge(s_pt, t + 1)
                if t < ML0:
                    pair, r = h // 2, FOX_HD * (h % 2)
                    if t == 0:
                        taken(pe, GROUP0[UNIT["fox_v"] + 1] - 1)
                        taken(pe, GROUP0[UNIT["fox_v"] + 1] - 2)
                    if pair >= 2:
                        pe.wait_ge(s_yfl, pair - 1)
                    for j in range(i + 1):
                        ins = pe.matmul(bank[6 + pair % 2][r:r + FOX_HD, P * i:P * i + P],
                                        fox_v[:, j, FOX_HD * h:FOX_HD * (h + 1)],
                                        prob_t[:, t % 2, P * j:P * j + P], start=(j == 0), stop=(j == i))
                else:
                    if h < 2:
                        pe.wait_ge(s_yfl, 3 + h)
                    else:
                        pe.wait_ge(s_mgate, h - 1)
                    taken(pe, GROUP0[UNIT["ml_v"] + 1] - 1)
                    taken(pe, GROUP0[UNIT["ml_v"] + 1] - 2)
                    for j in range(i + 1):
                        ins = pe.matmul(bank[6 + h % 2][:, P * i:P * i + P], prob_t[:, t % 2, P * j:P * j + P],
                                        ml_v[:, j, ML_HD * h:ML_HD * (h + 1)], start=(j == 0), stop=(j == i))
                ins.then_inc(s_value, 1)

            def ml_turn(h):
                pe.wait_ge(s_hm, h + 1)
                for i in range(NT):
                    ins = pe.transpose(bank[6 + h % 2][:, P * i:P * i + P], ml_h[:, P * i:P * i + P], ident[:])
                ins.then_inc(s_mturn, 1)

            def x_values(h):
                pe.wait_ge(s_pt, X0 + NT * (h + 1))
                n = UNIT[f"mem_v{h // 2}"]
                taken(pe, GROUP0[n] + 1)
                taken(pe, GROUP0[n])
                if 0 < h < X_HEADS - 1:
                    pe.wait_ge(s_ol, 2 * h)
                if h == X_HEADS - 1:
                    pe.wait_ge(s_exp, X0 + N_X)
                for d in range(2):
                    col = X_HD * h + P * d
                    for j in range(MEM // P):
                        ins = pe.matmul(x_bank(h, d)[:], mem_v[:, j, col:col + P], x_prob_t[:, h, j, :],
                                        start=(j == 0), stop=(j == 1))
                    ins.then_inc(s_xv, 1)

            pe.wait_ge(s_const, 1)
            for _ in range(WARM_UP):
                pe.matmul(bank[7][:, 0:P], ones[:], ones[:], start=True, stop=True)

            for step, n in steps:
                if step == "half":
                    half(n)
                elif step == "norm_turn":
                    norm_turn(n)
                elif step == "parameters":
                    pe.wait_ge(s_param, 16 * 4)
                    pe.transpose(bank[6][:, 0:n_param], param_rows[:], ident[0:n_param, 0:n_param])\
                      .then_inc(s_pturned, 1)
                elif step == "gates":
                    gates()
                elif step == "gate_turn":
                    pe.wait_ge(s_grows, 1)
                    for i in range(NT):
                        ins = pe.transpose(bank[7][:, 16 * i:16 * i + 16], gate_rows[:, P * i:P * i + P],
                                           ident[0:16, 0:16])
                    ins.then_inc(s_gturn, 1)
                elif step == "decay":
                    decays()
                elif step == "scores":
                    x_scores(n) if n >= X0 else scores(n)
                elif step == "turn":
                    turn(n)
                elif step == "values":
                    values(n)
                elif step == "ml_turn":
                    ml_turn(n)
                elif step == "x_values":
                    x_values(n)


N_SMALL = 6
N_CONST = 18


_INS = ["x", "mem", "norm_mix", "norm_xattn", "norm_mem", "norm_mlp", "w_in", "b_fox_f", "b_mlstm_i",
        "b_mlstm_f", "b_gate", "conv_w", "conv_b", "mlstm_norm", "w_up_fox", "w_up_mlstm", "w_mix_out",
        "w_xq", "w_xkv", "w_xo", "w_mlp_in", "w_mlp_out", "norm_final"]


def kernel(**inputs):
    import numpy as np
    import concourse.bacc as bacc
    from concourse.bass_utils import run_bass_kernel_spmd

    nc = bacc.Bacc("TRN2", target_bir_lowering=False, num_devices=1)
    arrays, args = {}, []
    for name in _INS:
        a = np.ascontiguousarray(inputs[name])
        if name != "norm_final":
            a = a[0]
        arrays[f"in_{name}"] = a
        args.append(nc.dram_tensor(f"in_{name}", a.shape, F32, kind="ExternalInput").ap())
    args.append(nc.dram_tensor("out_0", (TOK, DM), F32, kind="ExternalOutput").ap())
    trunk(nc, *args)
    r = run_bass_kernel_spmd(nc, [arrays], core_ids=[0])
    return r.results[0]["out_0"].reshape(1, TOK, DM)
```
